# Optimizing a Trainium2 kernel written in Bass

```python
import math
import jax, jax.numpy as jnp
from jax import lax
import numpy as np

D_MODEL = 1024
BATCH = 1
SEQ = 128
DEPTH = 2
DEC_BATCH = 1
DEC_SEQ = 512
PAST_LEN = 128

GRID_W = 64
F_GROUPS = 4
F_GROUP_DIM = 64
F_WIDTH = F_GROUPS * F_GROUP_DIM
MLA_HEADS = 8
QK_NOPE = 64
QK_ROPE = 32
V_DIM = 64
Q_LORA = 256
KV_LORA = 128
MLA_WIDTH = MLA_HEADS * V_DIM
GLA_HEADS = 4
GLA_DK = 32
GLA_DV = 64
GLA_WIDTH = GLA_HEADS * GLA_DV
GLA_GATE_RANK = 16
GLA_TAU = 16.0
GLA_CHUNK = 64
D_FF = 4 * D_MODEL
N_BRANCH = 3
ROPE_BASE = 10000.0
NORM_EPS = 1e-6
Q_BLOCK = 128
IN_SIZES = (F_WIDTH, Q_LORA, KV_LORA, QK_ROPE, GLA_HEADS * GLA_DK, GLA_HEADS * GLA_DK,
            GLA_WIDTH, GLA_WIDTH, GLA_GATE_RANK, GLA_GATE_RANK, N_BRANCH * D_MODEL)
D_IN = F_WIDTH + Q_LORA + KV_LORA + QK_ROPE + 2 * GLA_HEADS * GLA_DK + 2 * GLA_WIDTH + 2 * GLA_GATE_RANK + N_BRANCH * D_MODEL

kernel_name = 'hybrid_fourier_mla_gla_prefix_dit_step'

def rms_norm(x, g=None):
    xf = x.astype(jnp.float32)
    y = xf * lax.rsqrt(jnp.mean(xf * xf, axis=-1, keepdims=True) + NORM_EPS)
    if g is not None:
        y = y * g.astype(jnp.float32)
    return y.astype(x.dtype)

def split_cols(z, sizes):
    idx = [int(v) for v in np.cumsum(np.array(sizes))[:-1]]
    return jnp.split(z, idx, axis=-1)

def axial_rope(x):
    L = x.shape[1]
    rows = L // GRID_W
    row = jnp.repeat(jnp.arange(rows), GRID_W)
    col = jnp.tile(jnp.arange(GRID_W), rows)
    half = QK_ROPE // 2
    inv = ROPE_BASE ** (-jnp.arange(0, half, 2, dtype=jnp.float32) / half)

    def rot(xh, pos):
        ang = pos.astype(jnp.float32)[:, None] * inv[None, :]
        cos = jnp.cos(ang)[None, :, None, :]
        sin = jnp.sin(ang)[None, :, None, :]
        a, b = jnp.split(xh.astype(jnp.float32), 2, axis=-1)
        return jnp.concatenate([a * cos - b * sin, a * sin + b * cos], axis=-1)

    out = jnp.concatenate([rot(x[..., :half], row), rot(x[..., half:], col)], axis=-1)
    return out.astype(x.dtype)

def attend(q, k, v):
    B, L, H, dq = q.shape
    dv = v.shape[-1]
    blk = math.gcd(L, Q_BLOCK)
    n = L // blk
    qb = q.reshape(B, n, blk, H, dq).transpose(1, 0, 2, 3, 4)
    scale = dq ** -0.5

    def one(qi):
        s = jnp.einsum('bqhd,bkhd->bhqk', qi, k, preferred_element_type=jnp.float32) * scale
        p = jax.nn.softmax(s, axis=-1)
        return jnp.einsum('bhqk,bkhe->bqhe', p.astype(v.dtype), v)

    o = lax.map(one, qb)
    return o.transpose(1, 0, 2, 3, 4).reshape(B, L, H * dv)

def gla_chunked(q, k, v, log_a, s0):
    B, L, H, DK = q.shape
    DV = v.shape[-1]
    C = math.gcd(L, GLA_CHUNK)
    n = L // C

    def to_chunks(t):
        return t.reshape(B, n, C, H, t.shape[-1]).transpose(1, 0, 3, 2, 4)

    causal = jnp.tril(jnp.ones((C, C), dtype=bool))[None, None, :, :, None]

    def step(S, inp):
        qi, ki, vi, gi = inp
        b = jnp.cumsum(gi, axis=2)
        inter = jnp.einsum('bhid,bhde->bhie', qi * jnp.exp(b), S)
        diff = b[:, :, :, None, :] - b[:, :, None, :, :]
        decay = jnp.where(causal, jnp.exp(jnp.minimum(diff, 0.0)), 0.0)
        scores = jnp.einsum('bhid,bhjd,bhijd->bhij', qi, ki, decay)
        intra = jnp.einsum('bhij,bhje->bhie', scores, vi)
        b_last = b[:, :, -1:, :]
        S_new = jnp.exp(b_last[:, :, 0, :])[..., None] * S + jnp.einsum(
            'bhjd,bhje->bhde', ki * jnp.exp(b_last - b), vi)
        return S_new, inter + intra

    S_fin, o = lax.scan(step, s0, (to_chunks(q), to_chunks(k), to_chunks(v), to_chunks(log_a)))
    o = o.transpose(1, 0, 3, 2, 4).reshape(B, L, H, DV)
    return o, S_fin

def mixer(h, p, ctx):
    B, L, _ = h.shape
    z = h @ p['w_in']
    zf, zqd, zkvd, zkr, zgq, zgk, zgv, zgr, zaf, zab, zgate = split_cols(z, IN_SIZES)

    f = zf.reshape(B, L, F_GROUPS, F_GROUP_DIM).astype(jnp.float32)
    f = jnp.real(jnp.fft.fft2(f, axes=(1, 3), norm='ortho')).reshape(B, L, F_WIDTH).astype(h.dtype)
    y_a = f @ p['w_o_fourier']

    cq = rms_norm(zqd, p['mla_q_norm_g'])
    q = (cq @ p['w_q_up']).reshape(B, L, MLA_HEADS, QK_NOPE + QK_ROPE)
    ckv = rms_norm(zkvd, p['mla_kv_norm_g'])
    k_rope = zkr
    if ctx is None:
        q_att = q
        ckv_all, kr_all = ckv, k_rope
    else:
        q_att = jnp.concatenate([q[..., :QK_NOPE], axial_rope(q[..., QK_NOPE:])], axis=-1)
        kr_lat = axial_rope(k_rope[:, :, None, :])[:, :, 0, :]
        ckv_all = jnp.concatenate([ctx[0].astype(ckv.dtype), ckv], axis=1)
        kr_all = jnp.concatenate([ctx[1].astype(kr_lat.dtype), kr_lat], axis=1)
    Lk = ckv_all.shape[1]
    kv = (ckv_all @ p['w_kv_up']).reshape(B, Lk, MLA_HEADS, QK_NOPE + V_DIM)
    k_nope, v = kv[..., :QK_NOPE], kv[..., QK_NOPE:]
    k = jnp.concatenate(
        [k_nope, jnp.broadcast_to(kr_all[:, :, None, :], (B, Lk, MLA_HEADS, QK_ROPE))], axis=-1)
    y_b = attend(q_att, k, v) @ p['w_o_mla']

    f32 = jnp.float32
    gq = zgq.reshape(B, L, GLA_HEADS, GLA_DK).astype(f32) * (GLA_DK ** -0.5)
    gk = zgk.reshape(B, L, GLA_HEADS, GLA_DK).astype(f32)
    gv = zgv.reshape(B, L, GLA_HEADS, GLA_DV).astype(f32)
    la_f = jax.nn.log_sigmoid((zaf @ p['gla_wa2_f'] + p['gla_ba_f']).astype(f32)) / GLA_TAU
    la_b = jax.nn.log_sigmoid((zab @ p['gla_wa2_b'] + p['gla_ba_b']).astype(f32)) / GLA_TAU
    la_f = la_f.reshape(B, L, GLA_HEADS, GLA_DK)
    la_b = la_b.reshape(B, L, GLA_HEADS, GLA_DK)
    if ctx is None:
        s0_f = jnp.zeros((B, GLA_HEADS, GLA_DK, GLA_DV), f32)
        s0_b = jnp.zeros((B, GLA_HEADS, GLA_DK, GLA_DV), f32)
    else:
        s0_f = ctx[2].astype(f32)
        s0_b = ctx[3].astype(f32)
    o_f, s_f = gla_chunked(gq, gk, gv, la_f, s0_f)
    o_b, s_b = gla_chunked(jnp.flip(gq, 1), jnp.flip(gk, 1), jnp.flip(gv, 1), jnp.flip(la_b, 1), s0_b)
    o_g = rms_norm(o_f + jnp.flip(o_b, 1)).reshape(B, L, GLA_WIDTH) * p['gla_norm_g'].astype(f32)
    o_g = (o_g * jax.nn.silu(zgr.astype(f32))).astype(h.dtype)
    y_c = o_g @ p['w_o_gla']

    g = jax.nn.sigmoid(zgate.astype(f32)).astype(h.dtype).reshape(B, L, N_BRANCH, D_MODEL)
    merged = g[:, :, 0] * y_a + g[:, :, 1] * y_b + g[:, :, 2] * y_c
    out = merged @ p['w_out']
    return out, (ckv, k_rope, s_f.astype(h.dtype), s_b.astype(h.dtype))

def layer(x, cond, p, ctx):
    mod = (jax.nn.silu(cond) @ p['w_mod'] + p['b_mod'])[:, None, :]
    shift1, scale1, gate1, shift2, scale2, gate2 = jnp.split(mod, 6, axis=-1)
    h = rms_norm(x, p['norm1_g']) * (1 + scale1) + shift1
    out, ctx_out = mixer(h, p, ctx)
    x = x + gate1 * out
    h2 = rms_norm(x, p['norm2_g']) * (1 + scale2) + shift2
    x = x + gate2 * (jnp.square(jax.nn.relu(h2 @ p['w_ff1'])) @ p['w_ff2'])
    return x, ctx_out

def setup_inputs(seed: int = 0) -> dict:
    key = jax.random.key(seed)
    ks = jax.random.split(key, 32)

    def nrm(k, shape, s):
        return jax.random.normal(k, shape, jnp.float32) * s

    return {
        'x_prompt': nrm(ks[0], (BATCH, SEQ, D_MODEL), 1.0),
        'x_sample': nrm(ks[1], (DEC_BATCH, DEC_SEQ, D_MODEL), 1.0),
        'c': nrm(ks[2], (DEC_BATCH, D_MODEL), 1.0),
        'cache_mla_ckv': nrm(ks[3], (DEC_BATCH, DEPTH, PAST_LEN, KV_LORA), 1.0),
        'cache_mla_krope': nrm(ks[4], (DEC_BATCH, DEPTH, PAST_LEN, QK_ROPE), 1.0),
        'state_gla': nrm(ks[5], (DEC_BATCH, DEPTH, 2, GLA_HEADS, GLA_DK, GLA_DV), 0.3),
        'c_ctx': nrm(ks[6], (D_MODEL,), 1.0),
        'w_mod': nrm(ks[7], (DEPTH, D_MODEL, 6 * D_MODEL), D_MODEL ** -0.5),
        'b_mod': nrm(ks[8], (DEPTH, 6 * D_MODEL), 0.02),
        'norm1_g': 1.0 + nrm(ks[9], (DEPTH, D_MODEL), 0.05),
        'w_in': nrm(ks[10], (DEPTH, D_MODEL, D_IN), D_MODEL ** -0.5),
        'mla_q_norm_g': 1.0 + nrm(ks[11], (DEPTH, Q_LORA), 0.05),
        'mla_kv_norm_g': 1.0 + nrm(ks[12], (DEPTH, KV_LORA), 0.05),
        'w_q_up': nrm(ks[13], (DEPTH, Q_LORA, MLA_HEADS * (QK_NOPE + QK_ROPE)), Q_LORA ** -0.5),
        'w_kv_up': nrm(ks[14], (DEPTH, KV_LORA, MLA_HEADS * (QK_NOPE + V_DIM)), KV_LORA ** -0.5),
        'gla_wa2_f': nrm(ks[15], (DEPTH, GLA_GATE_RANK, GLA_HEADS * GLA_DK), GLA_GATE_RANK ** -0.5),
        'gla_ba_f': nrm(ks[16], (DEPTH, GLA_HEADS * GLA_DK), 0.5),
        'gla_wa2_b': nrm(ks[17], (DEPTH, GLA_GATE_RANK, GLA_HEADS * GLA_DK), GLA_GATE_RANK ** -0.5),
        'gla_ba_b': nrm(ks[18], (DEPTH, GLA_HEADS * GLA_DK), 0.5),
        'gla_norm_g': 1.0 + nrm(ks[19], (DEPTH, GLA_WIDTH), 0.05),
        'w_o_fourier': nrm(ks[20], (DEPTH, F_WIDTH, D_MODEL), F_WIDTH ** -0.5),
        'w_o_mla': nrm(ks[21], (DEPTH, MLA_WIDTH, D_MODEL), MLA_WIDTH ** -0.5),
        'w_o_gla': nrm(ks[22], (DEPTH, GLA_WIDTH, D_MODEL), GLA_WIDTH ** -0.5),
        'w_out': nrm(ks[23], (DEPTH, D_MODEL, D_MODEL), D_MODEL ** -0.5),
        'norm2_g': 1.0 + nrm(ks[24], (DEPTH, D_MODEL), 0.05),
        'w_ff1': nrm(ks[25], (DEPTH, D_MODEL, D_FF), D_MODEL ** -0.5),
        'w_ff2': nrm(ks[26], (DEPTH, D_FF, D_MODEL), D_FF ** -0.5),
        'final_norm_g': 1.0 + nrm(ks[27], (D_MODEL,), 0.05),
    }

def reference(x_prompt, x_sample, c, cache_mla_ckv, cache_mla_krope, state_gla, c_ctx,
              w_mod, b_mod, norm1_g, w_in, mla_q_norm_g, mla_kv_norm_g, w_q_up, w_kv_up,
              gla_wa2_f, gla_ba_f, gla_wa2_b, gla_ba_b, gla_norm_g, w_o_fourier, w_o_mla,
              w_o_gla, w_out, norm2_g, w_ff1, w_ff2, final_norm_g):
    xp = x_prompt
    xs = x_sample
    cond_ctx = c_ctx[None, :]
    ckv_list, kr_list, gla_list = [], [], []
    for l in range(DEPTH):
        p = dict(w_mod=w_mod[l], b_mod=b_mod[l], norm1_g=norm1_g[l], w_in=w_in[l],
                 mla_q_norm_g=mla_q_norm_g[l], mla_kv_norm_g=mla_kv_norm_g[l],
                 w_q_up=w_q_up[l], w_kv_up=w_kv_up[l], gla_wa2_f=gla_wa2_f[l],
                 gla_ba_f=gla_ba_f[l], gla_wa2_b=gla_wa2_b[l], gla_ba_b=gla_ba_b[l],
                 gla_norm_g=gla_norm_g[l], w_o_fourier=w_o_fourier[l], w_o_mla=w_o_mla[l],
                 w_o_gla=w_o_gla[l], w_out=w_out[l], norm2_g=norm2_g[l], w_ff1=w_ff1[l],
                 w_ff2=w_ff2[l])
        xp, (ckv_c, kr_c, sf_c, sb_c) = layer(xp, cond_ctx, p, None)
        ckv_list.append(ckv_c)
        kr_list.append(kr_c)
        gla_list.append(jnp.stack([sf_c, sb_c], axis=1))
        ctx = (cache_mla_ckv[:, l], cache_mla_krope[:, l], state_gla[:, l, 0], state_gla[:, l, 1])
        xs, _ = layer(xs, c, p, ctx)
    y_prompt = rms_norm(xp, final_norm_g)
    y_sample = rms_norm(xs, final_norm_g)
    new_mla_ckv = jnp.stack(ckv_list, axis=1)
    new_mla_krope = jnp.stack(kr_list, axis=1)
    new_state_gla = jnp.stack(gla_list, axis=1)
    return (y_prompt, y_sample, new_mla_ckv, new_mla_krope, new_state_gla)


_drawn_inputs = setup_inputs


def setup_inputs(seed=0):
    import zlib

    import numpy as np

    out = dict(_drawn_inputs(seed))
    spreads = {}
    factors = {'cache_mla_ckv': 3.905,
     'cache_mla_krope': 7.057,
     'state_gla': 8.0,
     'mla_q_norm_g': 8.0,
     'gla_norm_g': 3.444}
    for name, (base, spread) in spreads.items():
        noise = np.random.default_rng([zlib.crc32(name.encode()), seed]).standard_normal(out[name].shape)
        drawn = base * np.exp(spread * noise) if base else spread * noise
        out[name] = __import__('jax').numpy.asarray(drawn.astype(out[name].dtype))
    for name, factor in factors.items():
        out[name] = (out[name] * factor).astype(out[name].dtype)
    return out
```

```python
from contextlib import ExitStack

import numpy as np

import concourse.bass as bass
from concourse import mybir

ALU = mybir.AluOpType
ACT = mybir.ActivationFunctionType
AX = mybir.AxisListType
F32 = mybir.dt.float32
F32R = mybir.dt.float32r
U8 = mybir.dt.uint8

P = 128
D = 1024
KT = D // P
DEPTH = 2
CTX = 128
LAT = 512
TOK = CTX + LAT
HALF = TOK // 2
GRID_W = 64
EPS = 1e-6

F_W = 256
Q_LORA = 256
KV_LORA = 128
HEADS = 8
NOPE = 64
ROPE = 32
V_DIM = 64
KEYS = TOK + CTX
QK = NOPE + ROPE
ATT_SCALE = float(QK) ** -0.5

G_HEADS = 4
G_DK = 32
G_DV = 64
CH = 128
NCH = TOK // CH
LEVELS = [64, 32, 16, 8, 4, 2, 1, 0]
TAU = 16.0

MOD_TILES = 6 * KT
FRONT_TILES = 12
MIX_TILES = 4 * KT
OUT_TILES = KT
FF_BLOCKS = 4
FF_TILES = FF_BLOCKS * 2 * KT
TILES = MOD_TILES + FRONT_TILES + MIX_TILES + OUT_TILES + FF_TILES
FRONT0 = MOD_TILES
MIX0 = FRONT0 + FRONT_TILES
OUT0 = MIX0 + MIX_TILES
FF0 = OUT0 + OUT_TILES
RAW = 4
SPLIT = 2
OUTS = FRONT_TILES + 6 * KT + OUT_TILES + FF_TILES
O_MIX = FRONT_TILES
O_OUT = O_MIX + 6 * KT
O_FF = O_OUT + OUT_TILES

SM_WQ = 0
SM_WK = SM_WQ + 2 * HEADS * P
SM_WV = SM_WK + HEADS * NOPE
SM_WA = SM_WV + HEADS * V_DIM
SM_CKV = SM_WA + 2 * P
SM_KR = SM_CKV + CTX
SM_ST = SM_KR + CTX
SM_N = SM_ST + 2 * G_HEADS * G_DV

V_BMOD = 0
V_N1 = V_BMOD + MOD_TILES
V_N2 = V_N1 + KT
V_QG = V_N2 + KT
V_KVG = V_QG + 2
V_BA = V_KVG + 1
V_GG = V_BA + 2
V_N = V_GG + 2

C_ID = 0
C_ONE = C_ID + P
C_O128 = C_ONE + P
C_B64 = C_O128 + P
C_DC = C_B64 + P
C_DS = C_DC + P
C_XC = C_DS + P
C_XS = C_XC + P
C_COS = C_XS + P
C_SIN = C_COS + LAT
C_BM = C_SIN + LAT
C_N = C_BM + G_HEADS * G_DV

U_DFT = 0
U_ZFTOK = U_DFT + 2 * 4 * LAT
U_PQ = U_ZFTOK + NCH * F_W
U_ZFT = U_PQ + 4 * TOK
U_Q = 0
U_K = U_Q + 2 * TOK
U_V = U_K + 2 * KEYS
U_P = U_V + 6 * HEADS * V_DIM
U_PT = U_P + 3 * TOK
U_RT = U_PT + 2 * TOK
U_E = 0
U_QK = U_E + 2 * 2 * TOK
U_T = U_QK + 2 * 2 * TOK
U_KT = U_T + G_HEADS * TOK
U_QD = U_KT + 8 * P
U_N = 2 * KT * TOK
assert U_RT + 2 * LAT <= U_N + 2 * LAT and U_QD + 2 * TOK <= U_N and U_ZFT + 2 * TOK <= U_N

LINKS = (73, 23)


class Engine:

    def __init__(self, eng, per_layer, step=None):
        self.eng, self.per_layer, self.step = eng, per_layer, step
        self.n, self.terms, self.layer = 0, [], None

    def at(self, sem, n, *terms):
        per, start = self.per_layer[id(sem)]
        v = self.layer * per + (n + start)
        for reg, k in terms:
            v = reg * k + v
        return v

    def link(self, ins):
        self.n += 1
        ins.then_inc(self.step, 1)
        self.eng.wait_ge(self.step, self.at(self.step, self.n, *self.terms))

    def loop(self, count, links=0):
        return Loop(self, count, links)


class Loop:

    def __init__(self, e, count, links):
        self.e, self.count, self.links = e, count, links

    def __enter__(self):
        self.fori = self.e.eng.Fori(0, self.count)
        i = self.fori.__enter__()
        self.at = self.e.n
        self.e.terms.append((i, self.links))
        return i

    def __exit__(self, *a):
        assert a[0] or self.e.n - self.at == self.links, ("links", self.e.n - self.at)
        self.e.n = self.at + self.count * self.links
        self.e.terms.pop()
        return self.fori.__exit__(*a)


def build(nc, xT, cond, stream, small, vecs, table, dft, mask, yT, ckvT_out, krT_out, st_out, links):
    per_layer = {}
    at = [-(-nc.sbuf_base // 32) * 32]

    def sb(name, shape, dt=F32, size=4):
        t = nc.alloc_sbuf_tensor_at(name, shape, dt, offset=at[0])
        at[0] += -(-int(np.prod(shape[1:])) * size // 32) * 32
        return t

    with ExitStack() as ctx:
        x = sb("x", [P, KT, TOK])
        hh = sb("h_hi_parts", [P, KT, TOK], F32R)
        hl = sb("h_lo_parts", [P, KT, TOK], F32R)
        U = nc.alloc_sbuf_tensor_at("scratch", [P, U_N], F32, offset=at[0])
        uh = sb("hid_hi_parts", [P, KT, TOK], F32R)
        ul = sb("hid_lo_parts", [P, KT, TOK], F32R)
        M = sb("merged", [P, KT, TOK])
        raw = sb("w_raw", [P, RAW, KT, P])
        wh = sb("w_hi_parts", [P, SPLIT, KT, P], F32R)
        wl = sb("w_lo_parts", [P, SPLIT, KT, P], F32R)
        sm = sb("small_weights", [P, SM_N])
        vec = sb("vectors", [P, DEPTH * V_N + KT])
        vl = sb("layer_vectors", [P, V_N])
        cst = sb("tables", [P, C_N])
        msk = sb("level_masks", [P, len(LEVELS), P], U8, 1)
        cnd = sb("cond_raw", [P, KT, 2])
        cs = sb("cond_parts", [P, KT, 2, 2], F32R)
        csf = sb("cond_silu", [P, KT, 2])
        modv = sb("modulation", [P, 6 * KT, 2])
        aff = sb("norm_scales", [P, 2, KT, 2])
        zero_eps = sb("zero_and_eps", [P, 2])
        zero, eps = zero_eps[:, 0:1], zero_eps[:, 1:2]
        stat = sb("softmax_stats", [P, 3, 4])
        gdec = sb("chunk_decays", [P, 2, NCH])
        FB = sb("gate_prefix_sums", [P, 2, NCH, CH + 1])
        gvt = sb("gla_v_tok", [P, NCH, G_HEADS * G_DV])
        gqk = sb("gla_q_k", [P, 2, TOK])
        gr = sb("gla_r", [P, 2, TOK])
        lat = sb("low_rank_latents", [P, 2 * TOK + KEYS])
        assert at[0] <= nc.sbuf_usable_end, at[0] - nc.sbuf_usable_end
        ps = ctx.enter_context(nc.psum_tensor("ps", [P, 8, 512], F32))

        def sem(name, per=0, start=0):
            s = ctx.enter_context(nc.semaphore(name))
            per_layer[id(s)] = (per, start)
            return s

        raw_in = [sem(f"raw_in{j}", 4 * TILES) for j in range(RAW)]
        w_hi = sem("w_hi", 2 * TILES)
        w_ready = sem("w_ready", TILES, RAW)
        mm_done = sem("mm_done", TILES + 2 * KT)
        pair_free = [sem(f"pair_free{j}", OUTS // 2) for j in range(SPLIT)]
        layer_open = sem("layer_open", 1)
        mod_row = sem("mod_row", MOD_TILES // 4)
        mod_turned = sem("mod_turned", MOD_TILES // 4)
        mod_read = sem("mod_read", MOD_TILES // 4, 1)
        affine_ready = sem("affine_ready", 1)
        squared = sem("squared", 2)
        x_squared = sem("x_squared", KT)
        sums = sem("sums", 2)
        meansq = sem("meansq", 2)
        rstd = sem("rstd", 2)
        xhat = sem("xhat", 16)
        h_hi = sem("h_hi", 16)
        h_ready = sem("h_ready", 16)
        lora_sq = sem("lora_sq", 1)
        zf_turned = sem("zf_turned", 1)
        gv_turned = sem("gv_turned", 1)
        zf_tok_ready = sem("zf_tok_ready", 1)
        gv_tok_ready = sem("gv_tok_ready", 1)
        lora_ms = sem("lora_ms", 1)
        lora_rstd = sem("lora_rstd", 1)
        lora_ready = sem("lora_ready", 1)
        la_mm = sem("la_mm", 1)
        la_u_ready = sem("la_u_ready", 2)
        la_log = sem("la_log", 2)
        prefix_ready = sem("prefix_ready", 1)
        f_cols = sem("f_cols", 1)
        pq_act = sem("pq_act", 1)
        pq_dve = sem("pq_dve", 1)
        f_mm = sem("f_mm", 1)
        f_cat = sem("f_cat", 1)
        keys_copied = sem("keys_copied", 1)
        kr_ready = sem("kr_ready", 1)
        v_mm = sem("v_mm", 6)
        v_act = sem("v_act", 3)
        v_dve = sem("v_dve", 3)
        kq_mm = sem("kq_mm", 32)
        k_sb = sem("k_sb", 16)
        q_nope = sem("q_nope", 16)
        q_rope = sem("q_rope", 8)
        s_mm = sem("s_mm", 40)
        negmax = sem("negmax", 40)
        exp_done = sem("exp_done", 40)
        p_ready = sem("p_ready", 40)
        pt_mm = sem("pt_mm", 40)
        pt_sb = sem("pt_sb", 40)
        pv_mm = sem("pv_mm", 40)
        o_cat = sem("o_cat", 40)
        gd_diff = sem("gd_diff", 2)
        gd_exp = sem("gd_exp", 2)
        gd_ready = sem("gd_ready", 1)
        kt_mm = sem("kt_mm", 1)
        kt_sb = sem("kt_sb", 1)
        u_mm = sem("u_mm", 1)
        u_read = sem("u_read", 1)
        states_ready = sem("states_ready", 1)
        e_diff = sem("e_diff", 7)
        e_exp = sem("e_exp", 7)
        level_ready = sem("level_ready", 8)
        score_mm = sem("score_mm", 40)
        score_sb = sem("score_sb", 40)
        og_mm = sem("og_mm", 1)
        og_sb = sem("og_sb", 1)
        og_ms = sem("og_ms", 1)
        og_rstd = sem("og_rstd", 1)
        og_cat = sem("og_cat", 1)
        r_sig = sem("r_sig", 1)
        cat_hi = sem("cat_hi", 8)
        cat_ready = sem("cat_ready", 8)
        gate_scratch_free = sem("gate_scratch_free", 1 + KT)
        m_hi = sem("m_hi", 8)
        m_ready = sem("m_ready", 8)
        hid_sq = sem("hid_sq", 32)
        hid_hi = sem("hid_hi", 32)
        hid_ready = sem("hid_ready", 32)
        small_in = sem("small_in", 16)
        dft_in = sem("dft_in", 16)
        state_out = sem("state_out", 16)
        ckv_out = sem("ckv_out", 32)
        dve_step = sem("dve_step", links[0])
        act_step = sem("act_step", links[1])
        cond_in = sem("cond_in")
        start_in = sem("start_in")
        cond_sig = sem("cond_sig")
        cond_silu = sem("cond_silu")
        cond_hi = sem("cond_hi")
        cond_ready = sem("cond_ready")
        fin_sq = sem("fin_sq")
        fin_sum = sem("fin_sum")
        fin_ms = sem("fin_ms")
        fin_step = sem("fin_step")
        fin_ln = sem("fin_ln")
        fin_rstd = sem("fin_rstd")
        eps_set = sem("eps_set")
        waits_met = sem("waits_met")
        fin_y = sem("fin_y")
        y_out = sem("y_out")

        cq = lat[:, 0:2 * TOK].rearrange("p (t n) -> p t n", t=2)
        ckvT = lat[:, 2 * TOK:2 * TOK + KEYS]
        states = lat[:, 0:2048].rearrange("p (d c n) -> p d c n", d=2, c=4)
        G = lat[:, 0:3 * TOK].rearrange("p (b n) -> p b n", b=3)
        zfT = U[:, U_ZFT:U_ZFT + 2 * TOK].rearrange("p (t n) -> p t n", t=2)
        zf_tok = U[:, U_ZFTOK:U_ZFTOK + NCH * F_W].rearrange("p (c n) -> p c n", c=NCH)
        gvT = M[:, 2:4, :]
        misc = M[:, 4, :]
        la_u = (M[:, 5, :], M[:, 7, :])
        la_e = (M[:, 6, :], U[:, U_ZFT + 2 * TOK:U_ZFT + 3 * TOK])
        DFT = U[:, U_DFT:U_DFT + 8 * LAT].rearrange("p (a t n) -> p a t n", a=2, t=4)
        PQ = U[:, U_PQ:U_PQ + 4 * TOK].rearrange("p (a n) -> p a n", a=4)
        qb = U[:, U_Q:U_Q + 2 * TOK].rearrange("p (b n) -> p b n", b=2)
        kb = U[:, U_K:U_K + 2 * KEYS].rearrange("p (b n) -> p b n", b=2)
        v_tok = U[:, U_V:U_V + 6 * HEADS * V_DIM].rearrange("p (c n) -> p c n", c=6)
        pb = U[:, U_P:U_P + 3 * TOK].rearrange("p (b n) -> p b n", b=3)
        pT = U[:, U_PT:U_PT + 2 * TOK].rearrange("p (b n) -> p b n", b=2)
        rt = U[:, U_RT:U_RT + 2 * LAT].rearrange("p (b n) -> p b n", b=2)
        E = U[:, U_E:U_E + 4 * TOK].rearrange("p (b a n) -> p b a n", b=2, a=2)
        QKl = U[:, U_QK:U_QK + 4 * TOK].rearrange("p (b a n) -> p b a n", b=2, a=2)
        Ts = U[:, U_T:U_T + G_HEADS * TOK].rearrange("p (h n) -> p h n", h=G_HEADS)
        KTt = U[:, U_KT:U_KT + 8 * P].rearrange("p (d c n) -> p d c n", d=2, c=4)
        QD = U[:, U_QD:U_QD + 2 * TOK].rearrange("p (d n) -> p d n", d=2)
        KD = E[:, 0, :, :]
        OT, OSQ = E[:, 0, :, :], E[:, 1, :, :]
        OR = QKl[:, 0, :, :]
        mrow = gr[0:4, 0, 0:4 * P]
        R, tmp, hid = gqk[:, 0, :], gqk[:, 1, :], gr

        def tab(c, n=P, rows=slice(0, P)):
            return cst[rows, c:c + n]

        def halves(ap):
            return ap.rearrange("p (h n) -> p h n", h=2)

        def pair(o):
            return ps[:, 2 * (o % 2):2 * (o % 2) + 2, 0:HALF]

        def groups(o):
            p = pair(o)
            return ((0, p[:, 0, 0:CTX], slice(0, CTX)), (1, p[:, 0, CTX:HALF], slice(CTX, HALF)),
                    (1, p[:, 1, :], slice(HALF, TOK)))

        def level(buf, q, s, t):
            return buf[:, q, :].rearrange("p (c g t s) -> p c g t s", c=NCH, t=2, s=s)[:, :, :, t, :]

        def prefix(d, s, t, shift):
            return FB[:, d, :, shift:shift + CH].rearrange("p c (g t s) -> p c g t s", t=2, s=s)[:, :, :, t, :]

        def middle(d, s):
            m = FB[:, d, :, 0:CH].rearrange("p c (g t s) -> p c g t s", t=2, s=s)[:, :, :, 1, 0:1]
            return m.to_broadcast([P, NCH, CH // (2 * s), s])

        block = ctx.enter_context(nc.Block())


        @block.sync
        def _(sp):
            for j in range(RAW):
                sp.dma_start(raw[:, j, :, :].rearrange("p k n -> p (k n)"), stream[j]).then_inc(raw_in[j], 16)
            with sp.Fori(1, DEPTH * TILES // RAW) as i:
                for j in range(RAW):
                    sp.wait_ge(w_ready, i * RAW + (j + 1))
                    sp.dma_start(raw[:, j, :, :].rearrange("p k n -> p (k n)"),
                                 stream[i * RAW + j]).then_inc(raw_in[j], 16)
            for j in range(SPLIT):
                sp.wait_ge(w_ready, DEPTH * TILES + j + 1)
                sp.dma_start(raw[:, j, :, :].rearrange("p k n -> p (k n)"), stream[j]).then_inc(raw_in[j], 16)


        @block.gpsimd
        def _(pool):
            pool.dma_start(cnd[:, :, :], cond).then_inc(cond_in, 16)
            for dst, src in ((x[:, :, :], xT), (vec[:, :], vecs), (cst[:, :], table),
                             (M[:, 0:2, :].rearrange("p t n -> p (t n)")[:, 0:8 * CH], mask)):
                pool.dma_start(dst, src).then_inc(start_in, 16)
            e = Engine(pool, per_layer)
            with pool.Fori(0, DEPTH) as e.layer:
                pool.wait_ge(layer_open, e.at(layer_open, 1))
                pool.sem_inc(waits_met, 1)
                pool.dma_start(DFT.rearrange("p a t n -> p (a t n)"), dft).then_inc(dft_in, 16)
                pool.dma_start(sm[:, :], small[e.layer]).then_inc(small_in, 16)
                pool.wait_ge(lora_ready, e.at(lora_ready, 1))
                pool.sem_inc(waits_met, 1)
                pool.dma_start(ckvT_out[e.layer], ckvT[:, 0:CTX]).then_inc(ckv_out, 16)
                pool.dma_start(krT_out[e.layer], misc[64:96, 0:CTX]).then_inc(ckv_out, 16)
                pool.wait_ge(states_ready, e.at(states_ready, 1))
                pool.sem_inc(waits_met, 1)
                pool.dma_start(st_out[e.layer], states[:, :, 0, :]).then_inc(state_out, 16)
            for k in range(KT):
                pool.wait_ge(fin_y, k + 1)
                pool.dma_start(yT[:, k, :], M[:, k, :]).then_inc(y_out, 16)
            pool.wait_ge(y_out, 16 * KT)
            pool.wait_ge(ckv_out, DEPTH * 32)
            pool.wait_ge(state_out, DEPTH * 16)


        @block.tensor
        def _(pe):
            e = Engine(pe, per_layer)
            mm = nc.tensor.matmul

            def product(o, q, hi, lo, ks=range(KT), before=None):
                out = pair(o)
                for k in ks:
                    if before:
                        before(k)
                    for n, (w, a) in enumerate(((wh, hi), (wh, lo), (wl, hi))):
                        for h in range(2):
                            last = mm(out[:, h, :], w[:, q % 2, k, :], a[:, k, h * HALF:(h + 1) * HALF],
                                      start=(k == ks[0] and n == 0), stop=(k == ks[-1] and n == 2))
                last.then_inc(mm_done, 1)

            def tile_ready(idx, *terms):
                pe.wait_ge(w_ready, e.at(w_ready, idx + 1, *terms))

            def banks_read(o, *terms):
                pe.wait_ge(pair_free[o % 2], e.at(pair_free[o % 2], o // 2, *terms))

            def mean_square(n):
                pe.wait_ge(sums, e.at(sums, n))
                for h in range(2):
                    last = mm(ps[:, 4 + h, 0:HALF], tab(C_ONE), M[:, 0, h * HALF:(h + 1) * HALF],
                              start=True, stop=True)
                last.then_inc(meansq, 1)

            def turn(out, src, rows=P):
                return nc.tensor.transpose(out, src, tab(C_ID))

            pe.wait_ge(cond_ready, 1)
            with pe.Fori(0, DEPTH) as e.layer:
                pe.sem_inc(waits_met, 1)
                with e.loop(MOD_TILES // 4) as i:
                    for q in range(4):
                        tile_ready(q, (i, 4))
                        for k in range(2):
                            for n, w in enumerate((wh, wl)):
                                last = mm(ps[0:4, 7, :], cs[:, 2 * q + k, :, :].rearrange("p a c -> p (a c)"),
                                          w[:, q % 2, 4 * k:4 * k + 4, :].rearrange("p a n -> p (a n)"),
                                          start=(q == 0 and k == 0 and n == 0), stop=(q == 3 and k == 1 and n == 1))
                        last.then_inc(mm_done, 1)
                    pe.wait_ge(mod_row, e.at(mod_row, 1, (i, 1)))
                    pe.wait_ge(mod_read, e.at(mod_read, 0, (i, 1)))
                    pe.sem_inc(waits_met, 1)
                    for j in range(4):
                        last = nc.tensor.transpose(ps[:, 6, 4 * j:4 * j + 4], mrow[:, j * P:(j + 1) * P],
                                                   tab(C_ID, 4, slice(0, 4)))
                    last.then_inc(mod_turned, 1)
                mean_square(1)
                for q in range(FRONT_TILES):
                    tile_ready(FRONT0 + q)
                    if q >= 2:
                        banks_read(q)
                    product(q, q, hh, hl, before=(lambda k: pe.wait_ge(h_ready, e.at(h_ready, k + 1))) if q == 0 else None)

                pe.wait_ge(pair_free[0], e.at(pair_free[0], 1))
                pe.wait_ge(pair_free[1], e.at(pair_free[1], 1))
                for c in range(NCH):
                    for t in range(2):
                        last = turn(ps[:, 4 + c // 2, (c % 2) * 256 + t * P:(c % 2) * 256 + (t + 1) * P],
                                    zfT[:, t, c * CH:(c + 1) * CH])
                last.then_inc(zf_turned, 1)
                pe.wait_ge(pair_free[0], e.at(pair_free[0], FRONT_TILES // 2))
                pe.wait_ge(pair_free[1], e.at(pair_free[1], FRONT_TILES // 2))
                for c in range(NCH):
                    for t in range(2):
                        last = turn(ps[:, c // 2, (c % 2) * 256 + t * P:(c % 2) * 256 + (t + 1) * P],
                                    gvT[:, t, c * CH:(c + 1) * CH])
                last.then_inc(gv_turned, 1)
                pe.wait_ge(zf_tok_ready, e.at(zf_tok_ready, 1))
                pe.wait_ge(lora_sq, e.at(lora_sq, 1))
                for h in range(2):
                    cols = slice(h * HALF, (h + 1) * HALF)
                    for t in range(2):
                        mm(ps[:, 4 + h, 0:HALF], tab(C_ONE), M[:, t, cols], start=(t == 0), stop=(t == 1))
                    last = mm(ps[:, 6 + h, 0:HALF], tab(C_O128), M[:, 5, cols], start=True, stop=True)
                last.then_inc(lora_ms, 1)
                pe.wait_ge(gv_tok_ready, e.at(gv_tok_ready, 1))
                pe.wait_ge(small_in, e.at(small_in, 16))
                for d in range(2):
                    for h in range(2):
                        last = mm(ps[:, 2 * d + h, 0:HALF], sm[0:32, SM_WA + d * P:SM_WA + (d + 1) * P],
                                  misc[0:32, h * HALF:(h + 1) * HALF], start=True, stop=True)
                last.then_inc(la_mm, 1)
                pe.wait_ge(lora_ready, e.at(lora_ready, 1))
                pe.wait_ge(dft_in, e.at(dft_in, 16))
                for a in range(2):
                    for t in range(2):
                        for c in range(4):
                            mm(ps[:, 4 + 2 * a + t, :], zf_tok[:, c + 1, t * P:(t + 1) * P], DFT[:, a, c, :],
                               start=(c == 0), stop=(c == 3))
                pe.wait_ge(la_u_ready, e.at(la_u_ready, 2))
                for a in range(2):
                    for t in range(2):
                        last = mm(ps[:, 0, (2 * a + t) * P:(2 * a + t + 1) * P], zf_tok[:, 0, t * P:(t + 1) * P],
                                  tab(C_XC + a * P), start=True, stop=True)
                last.then_inc(f_cols, 1)
                pe.wait_ge(pq_act, e.at(pq_act, 1))
                pe.wait_ge(pq_dve, e.at(pq_dve, 1))
                for t in range(2):
                    for a in range(2):
                        mm(ps[:, 1 + t, :], tab(C_DC + a * P), PQ[:, 2 * a + t, CTX:TOK], start=(a == 0), stop=(a == 1))
                for t in range(2):
                    for a in range(2):
                        last = mm(ps[:, 3, t * P:(t + 1) * P], tab(C_DC + a * P), PQ[:, 2 * a + t, 0:CTX],
                                  start=(a == 0), stop=(a == 1))
                last.then_inc(f_mm, 1)
                pe.wait_ge(keys_copied, e.at(keys_copied, 1))
                pe.wait_ge(f_cat, e.at(f_cat, 1))
                for c in range(6):
                    mm(ps[:, (4 + c) % 8, :], ckvT[:, c * P:(c + 1) * P], sm[:, SM_WV:SM_WV + HEADS * V_DIM],
                             start=True, stop=True).then_inc(v_mm, 1)

                def query_key_part(h, p):
                    if p == 0 and h == 0:
                        pe.wait_ge(v_act, e.at(v_act, 3))
                        pe.wait_ge(v_dve, e.at(v_dve, 3))
                    elif p == 0:
                        pe.wait_ge(q_nope, e.at(q_nope, 2 * h))
                    elif p < 3:
                        pe.wait_ge(k_sb, e.at(k_sb, 2 * h + p))
                    else:
                        pe.wait_ge(q_nope, e.at(q_nope, 2 * h + 1))
                        pe.wait_ge(q_rope, e.at(q_rope, h + 1))
                    if p < 2:
                        last = mm(ps[0:NOPE, 4, 0:KEYS // 2], sm[:, SM_WK + h * NOPE:SM_WK + (h + 1) * NOPE],
                                  ckvT[:, p * KEYS // 2:(p + 1) * KEYS // 2], start=True, stop=True)
                    else:
                        cols = slice(CTX, TOK) if p == 2 else slice(0, CTX)
                        for t in range(2):
                            w = sm[:, SM_WQ + (t * HEADS + h) * P:SM_WQ + (t * HEADS + h + 1) * P]
                            last = mm(ps[:, 4, 0:LAT if p == 2 else CTX], w, cq[:, t, cols], start=(t == 0),
                                      stop=(t == 1))
                    last.then_inc(kq_mm, 1)

                def scores(h, i, n):
                    if n >= 2:
                        pe.wait_ge(exp_done, e.at(exp_done, n - 1))
                    if i == 0:
                        pe.wait_ge(q_nope, e.at(q_nope, 2 * h + 2))
                    b = 2 * (n % 2)
                    q = qb[0:QK, h % 2, i * P:(i + 1) * P]
                    if i == 0:
                        last = mm(ps[:, b, 0:CTX], q, kb[0:QK, h % 2, 0:CTX], start=True, stop=True)
                    else:
                        for j in range(2):
                            last = mm(ps[:, b + j, 0:HALF], q,
                                      kb[0:QK, h % 2, CTX + j * HALF:CTX + (j + 1) * HALF], start=True, stop=True)
                    last.then_inc(s_mm, 1)

                def turn_probs(n):
                    pe.wait_ge(p_ready, e.at(p_ready, n + 1))
                    if n >= 1:
                        pe.wait_ge(pt_sb, e.at(pt_sb, n))
                    for c in range(1 if n % 5 == 0 else 5):
                        last = turn(ps[:, 6 + c // 3, (c % 3) * P:(c % 3 + 1) * P], pb[:, n % 3, c * P:(c + 1) * P])
                    last.then_inc(pt_mm, 1)

                def values(n):
                    h, i = divmod(n, 5)
                    pe.wait_ge(pt_sb, e.at(pt_sb, n + 1))
                    if n >= 1:
                        pe.wait_ge(o_cat, e.at(o_cat, n))
                    r = 64 * (h % 2)
                    out = ps[r:r + 64, 5, 0:P]
                    cs_ = (0,) if i == 0 else range(1, 6)
                    for c in cs_:
                        src = pT[:, n % 2, (c - 1 if i else 0) * P:(c if i else 1) * P]
                        last = mm(out, v_tok[:, c, h * V_DIM:(h + 1) * V_DIM], src, start=(c == cs_[0]),
                                  stop=(c == cs_[-1]))
                    last.then_inc(pv_mm, 1)

                pe.wait_ge(kr_ready, e.at(kr_ready, 1))
                for p in range(4):
                    query_key_part(0, p)
                for n in range(5 * HEADS + 3):
                    h, i = divmod(n, 5)
                    if n < 5 * HEADS:
                        scores(h, i, n)
                    if 2 <= n < 5 * HEADS + 2:
                        turn_probs(n - 2)
                    if n >= 3:
                        values(n - 3)
                    if i < 4 and h + 1 < HEADS:
                        query_key_part(h + 1, i)

                pe.wait_ge(gd_ready, e.at(gd_ready, 1))
                for d, chunks in enumerate(((0, 1, 2, 3), (0, 2, 3, 4))):
                    for j, c in enumerate(chunks):
                        last = turn(ps[:, 4 + d, j * P:(j + 1) * P], KD[:, d, c * CH:(c + 1) * CH])
                last.then_inc(kt_mm, 1)
                pe.wait_ge(kt_sb, e.at(kt_sb, 1))
                pe.wait_ge(o_cat, e.at(o_cat, 5 * HEADS))
                for d, chunks in enumerate(((0, 1, 2, 3), (0, 2, 3, 4))):
                    for j, c in enumerate(chunks):
                        last = mm(ps[:, (6 + 2 * d + j // 2) % 8, (j % 2) * 256:(j % 2 + 1) * 256], KTt[:, d, j, :],
                                  gvt[:, c, :], start=True, stop=True)
                last.then_inc(u_mm, 1)
                pe.wait_ge(u_read, e.at(u_read, 1))
                for lv in range(8):
                    pe.wait_ge(level_ready, e.at(level_ready, lv + 1))
                    for j in range(5):
                        if lv >= 1:
                            pe.wait_ge(score_sb, e.at(score_sb, 5 * (lv - 1) + j + 1))
                        if lv == 7:
                            for h in (j,) if j < 4 else range(G_HEADS):
                                rows = slice(32 * h, 32 * h + 32)
                                out, cols = (ps[:, h, :], slice(CTX, TOK)) if j < 4 else (ps[:, 4 + h, 0:CH], slice(0, CTX))
                                last = mm(out, tab(C_ONE, P, rows), QKl[rows, lv % 2, 0, cols], start=True, stop=True)
                            last.then_inc(score_mm, 1)
                            continue
                        for h, c in ([(j, c) for c in range(1, NCH)] if j < 4 else [(h, 0) for h in range(G_HEADS)]):
                            rows = slice(32 * h, 32 * h + 32)
                            out = ps[:, h, (c - 1) * CH:c * CH] if c else ps[:, 4 + h, 0:CH]
                            last = mm(out, QKl[rows, lv % 2, 1, c * CH:(c + 1) * CH],
                                      QKl[rows, lv % 2, 0, c * CH:(c + 1) * CH], start=True, stop=True)
                        last.then_inc(score_mm, 1)
                pe.wait_ge(score_sb, e.at(score_sb, 40))
                pe.wait_ge(states_ready, e.at(states_ready, 1))
                for t in range(2):
                    for c in range(NCH):
                        out = ps[:, t, (c - 1) * CH:c * CH] if c else ps[:, 2, t * CH:(t + 1) * CH]
                        for h in (2 * t, 2 * t + 1):
                            r = 64 * (h % 2)
                            last = mm(out[r:r + 64, :], gvt[:, c, h * G_DV:(h + 1) * G_DV],
                                      Ts[:, h, c * CH:(c + 1) * CH], start=True, stop=True)
                        for d, slot in ((0, c - 1), (1, 4 - c)) if c else ():
                            w = states[:, d, slot, t * P:(t + 1) * P] if slot else                                 sm[:, SM_ST + d * 256 + t * P:SM_ST + d * 256 + (t + 1) * P]
                            last = mm(out, w, QD[:, d, c * CH:(c + 1) * CH], start=False, stop=True,
                                      skip_group_check=True)
                last.then_inc(og_mm, 1)
                pe.wait_ge(og_sb, e.at(og_sb, 1))
                for t in range(2):
                    for h in range(2):
                        last = mm(ps[:, 4 + 2 * t + h, 0:HALF], tab(C_B64), OSQ[:, t, h * HALF:(h + 1) * HALF],
                                  start=True, stop=True)
                last.then_inc(og_ms, 1)

                with e.loop(KT) as m:
                    for q in range(3):
                        tile_ready(MIX0 + q, (m, 4))
                        banks_read(O_MIX + q, (m, 3))
                        product(q, q, hh, hl)
                    tile_ready(MIX0 + 3, (m, 4))
                    pe.wait_ge(cat_ready, e.at(cat_ready, KT))
                    for b, ks in enumerate((range(0, 2), range(2, 6), range(6, 8))):
                        banks_read(O_MIX + 3 + b, (m, 3))
                        product(3 + b, 3, uh, ul, ks)
                for q in range(OUT_TILES):
                    tile_ready(OUT0 + q)
                    banks_read(O_OUT + q)
                    product(q, q, hh, hl, before=(lambda k: pe.wait_ge(m_ready, e.at(m_ready, k + 1))) if q == 0 else None)
                mean_square(2)
                with e.loop(FF_BLOCKS) as f:
                    for q in range(KT):
                        tile_ready(FF0 + q, (f, 2 * KT))
                        banks_read(O_FF + q, (f, KT))
                        product(q, q, hh, hl, before=(lambda k: pe.wait_ge(h_ready, e.at(h_ready, KT + k + 1))) if q == 0 else None)
                    for q in range(KT):
                        tile_ready(FF0 + KT + q, (f, 2 * KT))
                        banks_read(O_FF + KT + q, (f, KT))
                        product(q, q, uh, ul,
                                before=(lambda k: pe.wait_ge(hid_ready, e.at(hid_ready, k + 1, (f, KT)))) if q == 0 else None)
            pe.wait_ge(fin_sum, 1)
            for h in range(2):
                last = mm(ps[:, 4 + h, 0:HALF], tab(C_ONE), M[:, 0, h * HALF:(h + 1) * HALF], start=True, stop=True)
            last.then_inc(fin_ms, 1)


        @block.scalar
        def _(act):
            e = Engine(act, per_layer, act_step)
            fn = nc.scalar.activation
            copy = nc.scalar.copy

            def split_hi(idx, done, *terms):
                g = idx + SPLIT
                act.wait_ge(raw_in[g % RAW], e.at(raw_in[g % RAW], 16 * (g // RAW + 1), *((r, 4 * k[0]) for r, *k in terms)))
                act.wait_ge(mm_done, e.at(mm_done, done, *((r, k[1]) for r, *k in terms)))
                for n in range(2):
                    ks = slice(4 * n, 4 * n + 4)
                    copy(wh[:, g % SPLIT, ks, :], raw[:, g % RAW, ks, :]).then_inc(w_hi, 1)

            def squares(done):
                for n in range(2):
                    fn(M[:, 4 * n:4 * n + 4, :], x[:, 4 * n:4 * n + 4, :], ACT.Square).then_inc(done, 1)

            def norm(n):
                act.wait_ge(meansq, e.at(meansq, n + 1))
                rsqrt(halves(R), ps[:, 4:6, 0:HALF], e.link).then_inc(rstd, 1)
                shift = modv[:, 3 * n * KT:(3 * n + 1) * KT, :]
                for k in range(KT):
                    act.wait_ge(xhat, e.at(xhat, KT * n + k + 1))
                    for g, cols in ((0, slice(0, CTX)), (1, slice(CTX, TOK))):
                        ins = fn(M[:, k, cols], M[:, k, cols], ACT.Identity, bias=shift[:, k, g:g + 1],
                                 scale=aff[:, n, k, g:g + 1])
                    e.link(ins)
                    copy(hh[:, k, :], M[:, k, :]).then_inc(h_hi, 1)

            def rsqrt(dst, src, link):
                link(fn(dst, src, ACT.Ln, bias=eps))
                return fn(dst, dst, ACT.Exp, scale=-0.5)

            act.wait_ge(eps_set, 1)
            act.wait_ge(cond_in, 16)
            fn(csf[:, :, :], cnd[:, :, :], ACT.Sigmoid).then_inc(cond_sig, 1)
            act.wait_ge(cond_silu, 1)
            copy(cs[:, :, 0, :], csf[:, :, :]).then_inc(cond_hi, 1)
            for g in range(SPLIT):
                act.wait_ge(raw_in[g], 16)
                for n in range(2):
                    ks = slice(4 * n, 4 * n + 4)
                    copy(wh[:, g, ks, :], raw[:, g, ks, :]).then_inc(w_hi, 1)

            with act.Fori(0, DEPTH) as e.layer:
                act.wait_ge(layer_open, e.at(layer_open, 1))
                squares(squared)
                with e.loop(MOD_TILES // 4) as i:
                    for q in range(3):
                        split_hi(q, q + 1, (i, 4, 4))
                    act.wait_ge(mm_done, e.at(mm_done, 4, (i, 4)))
                    copy(mrow, ps[0:4, 7, :]).then_inc(mod_row, 1)
                    split_hi(3, 4, (i, 4, 4))
                act.wait_ge(affine_ready, e.at(affine_ready, 1))
                norm(0)

                for q in range(FRONT_TILES):
                    act.wait_ge(mm_done, e.at(mm_done, FRONT0 + q + 1))
                    dst = (zfT[:, 0, :], zfT[:, 1, :], cq[:, 0, :], cq[:, 1, :], ckvT[:, 0:TOK], misc, gqk[:, 0, :],
                           gqk[:, 1, :], gvT[:, 0, :], gvT[:, 1, :], gr[:, 0, :], gr[:, 1, :])[q]
                    scale = float(G_DK) ** -0.5 if q == 6 else 1.0
                    ins = fn(halves(dst), pair(q), ACT.Copy, scale=scale)
                    ins.then_inc(pair_free[q % 2], 1)
                    split_hi(FRONT0 + q, FRONT0 + q + 1)
                act.wait_ge(pair_free[0], e.at(pair_free[0], 6))
                act.wait_ge(pair_free[1], e.at(pair_free[1], 6))
                fn(M[:, 0:2, :], cq, ACT.Square, scale=2.0)
                fn(M[:, 5, :], ckvT[:, 0:TOK], ACT.Square).then_inc(lora_sq, 1)
                act.wait_ge(lora_ms, e.at(lora_ms, 1))
                for a in range(2):
                    ins = rsqrt(halves(M[:, 6 + a, :]), ps[:, 4 + 2 * a:6 + 2 * a, 0:HALF], e.link)
                ins.then_inc(lora_rstd, 1)
                act.wait_ge(lora_ready, e.at(lora_ready, 1))
                act.wait_ge(la_mm, e.at(la_mm, 1))
                for d in range(2):
                    fn(halves(la_e[d]), ps[:, 2 * d:2 * d + 2, 0:HALF], ACT.Abs, bias=vl[:, V_BA + d:V_BA + d + 1])
                    fn(halves(la_u[d]), ps[:, 2 * d:2 * d + 2, 0:HALF], ACT.Identity,
                             bias=vl[:, V_BA + d:V_BA + d + 1]).then_inc(la_u_ready, 1)
                for d in range(2):
                    act.wait_ge(la_u_ready, e.at(la_u_ready, d + 1))
                    e.link(fn(la_e[d], la_e[d], ACT.Exp, scale=-1.0))
                    fn(la_e[d], la_e[d], ACT.Ln, bias=1.0).then_inc(la_log, 1)
                act.wait_ge(f_cols, e.at(f_cols, 1))
                for a in range(2):
                    ins = copy(PQ[:, a, CTX:TOK], ps[:, 4 + a, :])
                ins.then_inc(pq_act, 1)
                copy(ckvT[:, TOK:KEYS], sm[:, SM_CKV:SM_CKV + CTX])
                for b in range(2):
                    copy(kb[64:96, b, 0:CTX], misc[64:96, 0:CTX])
                    ins = copy(kb[64:96, b, TOK:KEYS], sm[64:96, SM_KR:SM_KR + CTX])
                ins.then_inc(keys_copied, 1)
                for c in range(0, 6, 2):
                    act.wait_ge(v_mm, e.at(v_mm, c + 1))
                    copy(v_tok[:, c, :], ps[:, (4 + c) % 8, :]).then_inc(v_act, 1)

                def query_key_part(h, p):
                    act.wait_ge(kq_mm, e.at(kq_mm, 4 * h + p + 1))
                    if p < 2:
                        copy(kb[0:NOPE, h % 2, p * KEYS // 2:(p + 1) * KEYS // 2], ps[0:NOPE, 4, 0:KEYS // 2]).then_inc(k_sb, 1)
                    elif p == 2:
                        copy(qb[0:NOPE, h % 2, CTX:TOK], ps[0:NOPE, 4, :]).then_inc(q_nope, 1)
                    else:
                        copy(qb[0:QK, h % 2, 0:CTX], ps[0:QK, 4, 0:CTX]).then_inc(q_nope, 1)

                for p in range(4):
                    query_key_part(0, p)
                for n in range(5 * HEADS + 2):
                    h, i = divmod(n, 5)
                    if n < 5 * HEADS:
                        act.wait_ge(negmax, e.at(negmax, n + 1))
                        if n >= 3:
                            act.wait_ge(pt_mm, e.at(pt_mm, n - 2))
                        b = 2 * (n % 2)
                        src = ps[:, b:b + 2, 0:HALF] if i else ps[:, b:b + 1, 0:CTX]
                        dst = halves(pb[:, n % 3, :]) if i else pb[:, n % 3, 0:CTX].unsqueeze(1)
                        fn(dst, src, ACT.Exp, bias=stat[:, 0, n % 4:n % 4 + 1],
                                 accum_out=stat[:, 1, n % 4:n % 4 + 1]).then_inc(exp_done, 1)
                    if n >= 2:
                        m = n - 2
                        act.wait_ge(pt_mm, e.at(pt_mm, m + 1))
                        if m >= 2:
                            act.wait_ge(pv_mm, e.at(pv_mm, m - 1))
                        if m % 5:
                            copy(pT[:, m % 2, 0:3 * P], ps[:, 6, 0:3 * P])
                            ins = copy(pT[:, m % 2, 3 * P:5 * P], ps[:, 7, 0:2 * P])
                        else:
                            ins = copy(pT[:, m % 2, 0:P], ps[:, 6, 0:P])
                        ins.then_inc(pt_sb, 1)
                    if i < 4 and h + 1 < HEADS:
                        query_key_part(h + 1, i)

                act.wait_ge(gd_diff, e.at(gd_diff, 1))
                fn(KD[:, 0, :], KD[:, 0, :], ACT.Exp, scale=1 / TAU)
                fn(KD[:, 1, :].rearrange("p (c n) -> p c n", c=NCH), FB[:, 1, :, 0:CH], ACT.Exp, scale=1 / TAU).then_inc(gd_exp, 1)
                act.wait_ge(gd_diff, e.at(gd_diff, 2))
                fn(QD[:, 0, :].rearrange("p (c n) -> p c n", c=NCH), FB[:, 0, :, 1:CH + 1], ACT.Exp, scale=1 / TAU)
                fn(QD[:, 1, :], QD[:, 1, :], ACT.Exp, scale=1 / TAU)
                fn(gdec[:, :, :], FB[:, :, :, CH], ACT.Exp, scale=1 / TAU).then_inc(gd_exp, 1)
                for lv in range(7):
                    act.wait_ge(e_diff, e.at(e_diff, lv + 1))
                    fn(E[:, lv % 2, :, :], E[:, lv % 2, :, :], ACT.Exp, scale=1 / TAU).then_inc(e_exp, 1)
                act.wait_ge(og_mm, e.at(og_mm, 1))
                for f_, dst in ((ACT.Copy, OT), (ACT.Square, OSQ)):
                    for t in range(2):
                        fn(dst[:, t, CTX:TOK], ps[:, t, :], f_)
                    ins = fn(dst[:, :, 0:CTX], ps[:, 2, 0:2 * CTX].rearrange("p (t n) -> p t n", t=2), f_)
                ins.then_inc(og_sb, 1)
                act.wait_ge(og_ms, e.at(og_ms, 1))
                rsqrt(OR.rearrange("p t (h n) -> p (t h) n", h=2), ps[:, 4:8, 0:HALF], e.link).then_inc(og_rstd, 1)

                act.wait_ge(state_out, e.at(state_out, 16))
                act.wait_ge(og_cat, e.at(og_cat, 1))
                fn(G[:, 0:2, :], gr[:, :, :], ACT.Sigmoid).then_inc(r_sig, 1)
                for k in range(KT):
                    if k == 6:
                        act.wait_ge(gate_scratch_free, e.at(gate_scratch_free, 1))
                    copy(uh[:, k, :], M[:, k, :]).then_inc(cat_hi, 1)
                with e.loop(KT) as m:
                    act.wait_ge(gate_scratch_free, e.at(gate_scratch_free, 1, (m, 1)))
                    for q in range(3):
                        act.wait_ge(mm_done, e.at(mm_done, MIX0 + q + 1, (m, 6)))
                        fn(halves(G[:, q, :]), pair(q), ACT.Sigmoid).then_inc(pair_free[q % 2], 1)
                        split_hi(MIX0 + q, MIX0 + q + 1, (m, 4, 6))
                    split_hi(MIX0 + 3, MIX0 + 6, (m, 4, 6))
                act.wait_ge(gate_scratch_free, e.at(gate_scratch_free, 1 + KT))
                for k in range(KT):
                    copy(hh[:, k, :], M[:, k, :]).then_inc(m_hi, 1)
                for q in range(OUT_TILES):
                    split_hi(OUT0 + q, OUT0 + 2 * KT + q + 1)
                    act.wait_ge(pair_free[q % 2], e.at(pair_free[q % 2], (O_OUT + q) // 2 + 1))
                    fn(M[:, q, :], x[:, q, :], ACT.Square).then_inc(x_squared, 1)
                norm(1)
                with e.loop(FF_BLOCKS, 0) as f:
                    for q in range(KT):
                        done = FF0 + 2 * KT + q + 1
                        act.wait_ge(mm_done, e.at(mm_done, done, (f, 2 * KT)))
                        fn(halves(gqk[:, q % 2, :]), pair(q), ACT.Relu).then_inc(pair_free[q % 2], 1)
                        act.wait_ge(hid_sq, e.at(hid_sq, q + 1, (f, KT)))
                        copy(uh[:, q, :], hid[:, q % 2, :]).then_inc(hid_hi, 1)
                        split_hi(FF0 + q, done, (f, 2 * KT, 2 * KT))
                    for q in range(KT, 2 * KT):
                        split_hi(FF0 + q, FF0 + 2 * KT + q + 1, (f, 2 * KT, 2 * KT))
            for b in range(SPLIT):
                act.wait_ge(pair_free[b], DEPTH * OUTS // 2)
            squares(fin_sq)

            def link(ins):
                ins.then_inc(fin_ln, 1)
                act.wait_ge(fin_ln, 1)

            act.wait_ge(fin_ms, 1)
            rsqrt(halves(R), ps[:, 4:6, 0:HALF], link).then_inc(fin_rstd, 1)


        @block.vector
        def _(dve):
            e = Engine(dve, per_layer, dve_step)
            v = nc.vector
            tt, ts, stt, cp = v.tensor_tensor, v.tensor_scalar, v.scalar_tensor_tensor, v.tensor_copy

            def low(dst, full, hi):
                return tt(dst, full, hi.bitcast(F32), ALU.subtract)

            def split_lo(idx, *terms):
                g = idx + SPLIT
                for n in range(2):
                    ks = slice(4 * n, 4 * n + 4)
                    dve.wait_ge(w_hi, e.at(w_hi, 2 * g + n + 1, *((r, 2 * k) for r, k in terms)))
                    ins = low(wl[:, g % SPLIT, ks, :], raw[:, g % RAW, ks, :], wh[:, g % SPLIT, ks, :])
                ins.then_inc(w_ready, 1)

            def sum_tiles(link):
                link(tt(M[:, 0:4, :], M[:, 0:4, :], M[:, 4:8, :], ALU.add))
                link(tt(M[:, 0:2, :], M[:, 0:2, :], M[:, 2:4, :], ALU.add))
                return tt(M[:, 0, :], M[:, 0, :], M[:, 1, :], ALU.add)

            def norm(n):
                dve.wait_ge(rstd, e.at(rstd, n + 1))
                for k in range(KT + 2):
                    if k < KT:
                        tt(M[:, k, :], x[:, k, :], R, ALU.mult).then_inc(xhat, 1)
                    if k >= 2:
                        dve.wait_ge(h_hi, e.at(h_hi, KT * n + k - 1))
                        low(hl[:, k - 2, :], M[:, k - 2, :], hh[:, k - 2, :]).then_inc(h_ready, 1)

            def add_to_x(k, o, gate):
                for g, src, cols in groups(o):
                    ins = stt(x[:, k, cols], src, modv[:, gate * KT + k, g:g + 1], x[:, k, cols], ALU.mult, ALU.add)
                return ins

            v.memset(zero, 0.0)
            v.memset(eps, EPS).then_inc(eps_set, 1)
            dve.wait_ge(cond_in, 16)
            dve.wait_ge(cond_sig, 1)
            tt(csf[:, :, :], csf[:, :, :], cnd[:, :, :], ALU.mult).then_inc(cond_silu, 1)
            dve.wait_ge(cond_hi, 1)
            low(cs[:, :, 1, :], csf[:, :, :], cs[:, :, 0, :]).then_inc(cond_ready, 1)
            for g in range(SPLIT):
                dve.wait_ge(w_hi, 2 * g + 2)
                ins = low(wl[:, g, :, :], raw[:, g, :, :], wh[:, g, :, :])
                ins.then_inc(w_ready, 1 + RAW // SPLIT)
            dve.wait_ge(start_in, 64)
            ins = cp(msk[:, :, :].rearrange("p l n -> p (l n)"), M[:, 0:2, :].rearrange("p t n -> p (t n)")[:, 0:8 * CH])
            ins.then_inc(mod_read, 1)

            with dve.Fori(0, DEPTH) as e.layer:
                v.memset(FB[:, :, :, 0], 0.0).then_inc(layer_open, 1)
                e.link(cp(vl[:, :], vec[:, bass.ds(e.layer * V_N, V_N)]))
                dve.wait_ge(squared, e.at(squared, 2))
                sum_tiles(e.link).then_inc(sums, 1)
                with e.loop(MOD_TILES // 4) as i:
                    for q in range(4):
                        split_lo(q, (i, 4))
                    dve.wait_ge(mod_turned, e.at(mod_turned, 1, (i, 1)))
                    v.tensor_reduce(modv[:, bass.ds(i * 4, 4), :], ps[:, 6, 0:16].rearrange("p (j a c) -> p j c a", a=2, c=2),
                                    AX.X, ALU.add).then_inc(mod_read, 1)
                dve.wait_ge(mod_read, e.at(mod_read, MOD_TILES // 4))
                e.link(tt(modv[:, :, :], modv[:, :, :],
                          vl[:, V_BMOD:V_BMOD + MOD_TILES].unsqueeze(2).to_broadcast([P, MOD_TILES, 2]), ALU.add))
                for n, c in ((0, V_N1), (1, V_N2)):
                    ins = stt(aff[:, n, :, :], modv[:, (3 * n + 1) * KT:(3 * n + 2) * KT, :], 1.0,
                              vl[:, c:c + KT].unsqueeze(2).to_broadcast([P, KT, 2]), ALU.add, ALU.mult)
                ins.then_inc(affine_ready, 1)
                dve.wait_ge(rstd, e.at(rstd, 1))
                for k in range(KT + 2):
                    if k < KT:
                        tt(M[:, k, :], x[:, k, :], R, ALU.mult).then_inc(xhat, 1)
                    if k >= 2:
                        dve.wait_ge(h_hi, e.at(h_hi, k - 1))
                        low(hl[:, k - 2, :], M[:, k - 2, :], hh[:, k - 2, :]).then_inc(h_ready, 1)
                for q in range(FRONT_TILES):
                    split_lo(FRONT0 + q)

                dve.wait_ge(zf_turned, e.at(zf_turned, 1))
                for b in range(3):
                    ins = cp(zf_tok[:, 2 * b:min(2 * b + 2, NCH), :].rearrange("p c n -> p (c n)"),
                             ps[:, 4 + b, 0:512 if b < 2 else 256])
                ins.then_inc(zf_tok_ready, 1)
                dve.wait_ge(gv_turned, e.at(gv_turned, 1))
                for b in range(3):
                    ins = cp(gvt[:, 2 * b:min(2 * b + 2, NCH), :].rearrange("p c n -> p (c n)"),
                             ps[:, b, 0:512 if b < 2 else 256])
                ins.then_inc(gv_tok_ready, 1)
                dve.wait_ge(lora_rstd, e.at(lora_rstd, 1))
                e.link(ts(M[:, 6, :], M[:, 6, :], ATT_SCALE, None, ALU.mult))
                for t in range(2):
                    stt(cq[:, t, :], cq[:, t, :], vl[:, V_QG + t:V_QG + t + 1], M[:, 6, :], ALU.mult, ALU.mult)
                stt(ckvT[:, 0:TOK], ckvT[:, 0:TOK], vl[:, V_KVG:V_KVG + 1], M[:, 7, :], ALU.mult, ALU.mult).then_inc(lora_ready, 1)
                for d in range(2):
                    dve.wait_ge(la_log, e.at(la_log, d + 1))
                    e.link(stt(la_u[d], la_u[d], 0.0, la_e[d], ALU.min, ALU.subtract))
                for d in range(2):
                    for c in range(NCH):
                        ins = v.tensor_tensor_scan(FB[:, d, c, 1:CH + 1], la_u[d][:, c * CH:(c + 1) * CH],
                                                   zero.to_broadcast([P, CH]), 0.0, ALU.add, ALU.min)
                ins.then_inc(prefix_ready, 1)
                dve.wait_ge(f_cols, e.at(f_cols, 1))
                for a in range(2, 4):
                    cp(PQ[:, a, CTX:TOK], ps[:, 4 + a, :])
                cp(PQ[:, :, 0:CTX], ps[:, 0, :].rearrange("p (a n) -> p a n", a=4)).then_inc(pq_dve, 1)
                dve.wait_ge(f_mm, e.at(f_mm, 1))
                for t in range(2):
                    cp(M[:, t, CTX:TOK], ps[:, 1 + t, :])
                cp(M[:, 0:2, 0:CTX], ps[:, 3, 0:2 * CTX].rearrange("p (t n) -> p t n", t=2)).then_inc(f_cat, 1)
                tt(rt[64:96, 0, :], misc[64:96, CTX:TOK], tab(C_COS, LAT, slice(64, 96)), ALU.mult)
                e.link(tt(rt[64:96, 1, :], misc[96:128, CTX:TOK], tab(C_SIN, LAT, slice(96, 128)), ALU.mult))
                for b in range(2):
                    ins = tt(kb[64:96, b, CTX:TOK], rt[64:96, 0, :], rt[64:96, 1, :], ALU.add)
                ins.then_inc(kr_ready, 1)
                for c in range(1, 6, 2):
                    dve.wait_ge(v_mm, e.at(v_mm, c + 1))
                    cp(v_tok[:, c, :], ps[:, (4 + c) % 8, :]).then_inc(v_dve, 1)

                def rope(h):
                    dve.wait_ge(kq_mm, e.at(kq_mm, 4 * h + 3))
                    tt(rt[64:96, 0, :], ps[64:96, 4, :], tab(C_COS, LAT, slice(64, 96)), ALU.mult)
                    e.link(tt(rt[64:96, 1, :], ps[96:128, 4, :], tab(C_SIN, LAT, slice(96, 128)), ALU.mult))
                    tt(qb[64:96, h % 2, CTX:TOK], rt[64:96, 0, :], rt[64:96, 1, :], ALU.add).then_inc(q_rope, 1)

                rope(0)
                dve.wait_ge(ckv_out, e.at(ckv_out, 32))
                for n in range(5 * HEADS + 4):
                    h, i = divmod(n, 5)
                    if n >= 4:
                        m = n - 4
                        hm, im = divmod(m, 5)
                        dve.wait_ge(pv_mm, e.at(pv_mm, m + 1))
                        r = 64 * (hm % 2)
                        cp(M[r:r + 64, 2 + hm // 2, im * P:(im + 1) * P],
                                 ps[r:r + 64, 5, 0:P]).then_inc(o_cat, 1)
                    if n < 5 * HEADS:
                        dve.wait_ge(s_mm, e.at(s_mm, n + 1))
                        b = 2 * (n % 2)
                        src = ps[:, b:b + 2, 0:HALF] if i else ps[:, b:b + 1, 0:CTX]
                        v.tensor_reduce(stat[:, 0, n % 4:n % 4 + 1], src, AX.XY, ALU.max, negate=True).then_inc(negmax, 1)
                    if 1 <= n <= 5 * HEADS:
                        m = n - 1
                        dve.wait_ge(exp_done, e.at(exp_done, m + 1))
                        e.link(v.reciprocal(stat[:, 2, m % 4:m % 4 + 1], stat[:, 1, m % 4:m % 4 + 1]))
                        p = pb[:, m % 3, 0:TOK if m % 5 else CTX]
                        ts(p, p, stat[:, 2, m % 4:m % 4 + 1], None, ALU.mult).then_inc(p_ready, 1)
                    if i == 2 and h + 1 < HEADS:
                        rope(h + 1)

                for d, dst, lo_ in ((0, KD[:, 0, :], 1), (1, QD[:, 1, :], 0)):
                    tt(dst.rearrange("p (c n) -> p c n", c=NCH),
                             FB[:, d, :, CH:CH + 1].to_broadcast([P, NCH, CH]), FB[:, d, :, lo_:lo_ + CH], ALU.subtract).then_inc(gd_diff, 1)
                dve.wait_ge(gd_exp, e.at(gd_exp, 1))
                tt(KD, KD, gqk[:, 1:2, :].to_broadcast([P, 2, TOK]), ALU.mult).then_inc(gd_ready, 1)
                dve.wait_ge(gd_exp, e.at(gd_exp, 2))
                tt(QD, QD, gqk[:, 0:1, :].to_broadcast([P, 2, TOK]), ALU.mult)
                dve.wait_ge(kt_mm, e.at(kt_mm, 1))
                for d in range(2):
                    ins = cp(KTt[:, d, :, :].rearrange("p c n -> p (c n)"), ps[:, 4 + d, :])
                ins.then_inc(kt_sb, 1)

                def differences(lv):
                    s, b = LEVELS[lv], lv % 2
                    if lv >= 2:
                        dve.wait_ge(level_ready, e.at(level_ready, lv - 1))
                    tt(level(E[:, b], 0, s, 1), prefix(0, s, 1, 1), middle(0, s), ALU.subtract)
                    tt(level(E[:, b], 0, s, 0), middle(1, s), prefix(1, s, 0, 0), ALU.subtract)
                    tt(level(E[:, b], 1, s, 0), middle(0, s), prefix(0, s, 0, 1), ALU.subtract)
                    tt(level(E[:, b], 1, s, 1), prefix(1, s, 1, 0), middle(1, s), ALU.subtract).then_inc(e_diff, 1)

                differences(0)
                differences(1)
                dve.wait_ge(e_exp, e.at(e_exp, 1))
                tt(QKl[:, 0, :, :], E[:, 0, :, :], gqk[:, :, :], ALU.mult).then_inc(level_ready, 1)
                dve.wait_ge(u_mm, e.at(u_mm, 1))
                own = tab(C_BM, 256)
                for d in range(2):
                    for j in range(4):
                        slot = j if d == 0 or j == 0 else 4 - j
                        u = ps[:, (6 + 2 * d + j // 2) % 8, (j % 2) * 256:(j % 2 + 1) * 256]
                        ins = tt(states[:, d, slot, :], u, own, ALU.mult)
                ins.then_inc(u_read, 1)
                dve.wait_ge(u_read, e.at(u_read, 1))
                for slot in (1, 2, 3):
                    for d in range(2):
                        c = slot if d == 0 else 5 - slot
                        old = states[:, d, slot - 1, :] if slot > 1 else sm[:, SM_ST + d * 256:SM_ST + (d + 1) * 256]
                        ins = stt(states[:, d, slot, :], old, gdec[:, d, c:c + 1], states[:, d, slot, :],
                                  ALU.mult, ALU.add)
                    if slot < 3:
                        e.link(ins)
                ins.then_inc(states_ready, 1)
                for lv in range(1, 9):
                    if lv < 6:
                        differences(lv + 1)
                    if lv < 8:
                        if lv >= 2:
                            dve.wait_ge(score_mm, e.at(score_mm, 5 * (lv - 1)))
                        if lv < 7:
                            dve.wait_ge(e_exp, e.at(e_exp, lv + 1))
                            ins = tt(QKl[:, lv % 2, :, :], E[:, lv % 2, :, :], gqk[:, :, :], ALU.mult)
                        else:
                            ins = stt(QKl[:, lv % 2, 0, :], gqk[:, 0, :], 2.0 * D, gqk[:, 1, :], ALU.mult, ALU.mult)
                        ins.then_inc(level_ready, 1)
                    if lv >= 1:
                        for j in range(5):
                            dve.wait_ge(score_mm, e.at(score_mm, 5 * (lv - 1) + j + 1))
                            dve.sem_inc(waits_met, 1)
                            if j < 4:
                                dst = Ts[:, j, CTX:TOK].rearrange("p (c n) -> p c n", n=CH)
                                src = ps[:, j, :].rearrange("p (c n) -> p c n", n=CH)
                            else:
                                dst, src = Ts[:, :, 0:CTX], ps[:, 4:8, 0:CTX]
                            if lv == 1:
                                ins = cp(dst, src)
                            else:
                                ins = v.copy_predicated(
                                    dst, msk[:, lv - 1:lv, :].to_broadcast([P, 4, CH]), src)
                            ins.then_inc(score_sb, 1)
                dve.wait_ge(og_rstd, e.at(og_rstd, 1))
                for t in range(2):
                    ins = stt(M[:, 6 + t, :], OT[:, t, :], vl[:, V_GG + t:V_GG + t + 1], OR[:, t, :], ALU.mult, ALU.mult)
                ins.then_inc(og_cat, 1)
                dve.wait_ge(r_sig, e.at(r_sig, 1))
                e.link(tt(gr[:, :, :], gr[:, :, :], G[:, 0:2, :], ALU.mult))
                tt(M[:, 6:8, :], M[:, 6:8, :], gr[:, :, :], ALU.mult).then_inc(gate_scratch_free, 1)
                for k in range(KT):
                    dve.wait_ge(cat_hi, e.at(cat_hi, k + 1))
                    low(ul[:, k, :], M[:, k, :], uh[:, k, :]).then_inc(cat_ready, 1)
                with e.loop(KT, 1) as m:
                    for q in range(3):
                        split_lo(MIX0 + q, (m, 4))
                    out = M[:, bass.ds(m, 1), :].rearrange("p a (h n) -> p (a h) n", h=2)
                    for b in range(3):
                        dve.wait_ge(pair_free[b % 2], e.at(pair_free[b % 2], (O_MIX + b) // 2 + 1, (m, 3)))
                        dve.wait_ge(mm_done, e.at(mm_done, MIX0 + 4 + b, (m, 6)))
                        dst = out if b == 0 else halves(tmp)
                        tt(dst, pair(3 + b), halves(G[:, b, :]), ALU.mult).then_inc(pair_free[(3 + b) % 2], 1)
                        dve.wait_ge(pair_free[(3 + b) % 2], e.at(pair_free[(3 + b) % 2], (O_MIX + 3 + b) // 2 + 1, (m, 3)))
                        if b == 1:
                            e.link(tt(out, out, halves(tmp), ALU.add))
                        if b == 2:
                            tt(out, out, halves(tmp), ALU.add).then_inc(gate_scratch_free, 1)
                    split_lo(MIX0 + 3, (m, 4))
                for k in range(KT):
                    dve.wait_ge(m_hi, e.at(m_hi, k + 1))
                    low(hl[:, k, :], M[:, k, :], hh[:, k, :]).then_inc(m_ready, 1)
                for q in range(OUT_TILES):
                    dve.wait_ge(mm_done, e.at(mm_done, OUT0 + 2 * KT + q + 1))
                    add_to_x(q, q, 2).then_inc(pair_free[q % 2], 1)
                    split_lo(OUT0 + q)
                    if q >= 1:
                        dve.wait_ge(x_squared, e.at(x_squared, q + 1))
                        ins = tt(M[:, 0, :], M[:, 0, :], M[:, q, :], ALU.add)
                        if q < OUT_TILES - 1:
                            e.link(ins)
                ins.then_inc(sums, 1)
                norm(1)
                with e.loop(FF_BLOCKS, 0) as f:
                    for q in range(KT):
                        dve.wait_ge(w_ready, e.at(w_ready, FF0 + q + 2, (f, 2 * KT)))
                        dve.wait_ge(pair_free[q % 2], e.at(pair_free[q % 2], (O_FF + q) // 2 + 1, (f, KT)))
                        tt(hid[:, q % 2, :], gqk[:, q % 2, :], gqk[:, q % 2, :], ALU.mult).then_inc(hid_sq, 1)
                        dve.wait_ge(hid_hi, e.at(hid_hi, q + 1, (f, KT)))
                        low(ul[:, q, :], hid[:, q % 2, :], uh[:, q, :]).then_inc(hid_ready, 1)
                        split_lo(FF0 + q, (f, 2 * KT))
                    for q in range(KT):
                        dve.wait_ge(mm_done, e.at(mm_done, FF0 + 2 * KT + KT + q + 1, (f, 2 * KT)))
                        add_to_x(q, q, 5).then_inc(pair_free[q % 2], 1)
                        split_lo(FF0 + KT + q, (f, 2 * KT))
            dve.wait_ge(fin_sq, 2)
            n = [0]

            def link(ins):
                n[0] += 1
                ins.then_inc(fin_step, 1)
                dve.wait_ge(fin_step, n[0])

            sum_tiles(link).then_inc(fin_sum, 1)
            dve.wait_ge(fin_rstd, 1)
            for k in range(KT):
                g = vec[:, DEPTH * V_N + k:DEPTH * V_N + k + 1]
                stt(M[:, k, :], x[:, k, :], g, R, ALU.mult, ALU.mult).then_inc(fin_y, 1)



def constants():
    t = np.zeros((P, C_N))
    t[:, C_ID:C_ID + P] = np.eye(P)
    t[:, C_ONE:C_ONE + P] = 1.0 / D
    t[:, C_O128:C_O128 + P] = 1.0 / KV_LORA
    g = np.arange(P) // 64
    same = g[:, None] == g[None, :]
    t[:, C_B64:C_B64 + P] = same / 64.0
    w = 2 * np.pi * np.outer(np.arange(P) % 64, np.arange(P) % 64) / 64
    t[:, C_DC:C_DC + P] = np.cos(w) * same
    t[:, C_DS:C_DS + P] = -np.sin(w) * same

    def dft(n):
        a = 2 * np.pi * (np.outer(np.arange(n), np.arange(n)) % n) / n
        return np.stack([np.cos(a), np.sin(a)]) / np.sqrt(n * 64)

    t[:, C_XC:C_XC + P], t[:, C_XS:C_XS + P] = dft(CTX)
    long = dft(LAT).reshape(2, 4, P, LAT).transpose(2, 0, 1, 3).reshape(P, 8 * LAT)
    half = ROPE // 2
    inv = (10000.0 ** (-np.arange(0, half, 2, dtype=np.float32) / half)).astype(np.float32)
    pos = np.stack([np.arange(LAT) // GRID_W, np.arange(LAT) % GRID_W]).astype(np.float32)
    r = np.arange(P) % ROPE
    ang = (pos[r // half] * inv[r % 8][:, None]).astype(np.float32).astype(np.float64)
    t[:, C_COS:C_COS + LAT] = np.cos(ang)
    t[:, C_SIN:C_SIN + LAT] = np.sin(ang) * np.where((r % half) < 8, -1.0, 1.0)[:, None]
    t[:, C_BM:C_BM + 256] = (np.arange(P) // G_DK)[:, None] == (np.arange(256) // G_DV)[None, :]
    i = np.arange(CH)
    m = np.zeros((P, len(LEVELS), CH), np.float32)
    for n, s in enumerate(LEVELS):
        if s:
            m[:, n] = (i[:, None] // (2 * s) == i[None, :] // (2 * s)) & (i[:, None] // s != i[None, :] // s)
        else:
            m[:, n] = i[:, None] == i[None, :]
    return t.astype(np.float32), long.astype(np.float32), m.reshape(P, -1)


def layer_inputs(w, l):
    def tile(mat):
        return mat.reshape(KT, P, P).transpose(1, 0, 2).reshape(P, KT * P)

    def cols(mat, n):
        return [tile(mat[:, P * j:P * (j + 1)]) for j in range(n)]

    win = w["w_in"][l]
    zf, qd, kvd, kr, gq, gk, gv, gr, za, gate = np.split(win, np.cumsum([256, 256, 128, 32, 128, 128, 256, 256, 32]), 1)
    other = np.concatenate([kr[:, 8:16], kr[:, 0:8], kr[:, 24:32], kr[:, 16:24]], 1)
    mod = w["w_mod"][l].reshape(4, 2, P, MOD_TILES // 4, 4 * P).transpose(3, 0, 2, 1, 4)
    tiles = list(mod.reshape(MOD_TILES, P, KT * P))
    tiles += cols(np.concatenate([zf, qd, kvd, za, za, kr, other, gq, gk, gv, gr], 1), FRONT_TILES)
    wo = np.concatenate([w["w_o_fourier"][l], w["w_o_mla"][l], w["w_o_gla"][l]], 0)
    for m in range(KT):
        tiles += [tile(gate[:, b * D + P * m:b * D + P * (m + 1)]) for b in range(3)]
        tiles += [tile(wo[:, P * m:P * (m + 1)])]
    tiles += cols(w["w_out"][l], KT)
    for f in range(FF_BLOCKS):
        tiles += cols(w["w_ff1"][l][:, D * f:D * (f + 1)], KT) + cols(w["w_ff2"][l][D * f:D * (f + 1)], KT)

    small = np.zeros((P, SM_N), np.float32)
    q = w["w_q_up"][l].reshape(2, P, HEADS, QK).transpose(1, 0, 2, 3)
    q = np.concatenate([q, q[..., 72:80], q[..., 64:72], q[..., 88:96], q[..., 80:88]], -1)
    small[:, SM_WQ:SM_WK] = q.reshape(P, 2 * HEADS * P)
    kv = w["w_kv_up"][l].reshape(KV_LORA, HEADS, NOPE + V_DIM)
    small[:, SM_WK:SM_WV] = kv[:, :, :NOPE].reshape(P, HEADS * NOPE)
    small[:, SM_WV:SM_WA] = kv[:, :, NOPE:].reshape(P, HEADS * V_DIM)
    small[0:16, SM_WA:SM_WA + P] = w["gla_wa2_f"][l]
    small[16:32, SM_WA + P:SM_WA + 2 * P] = w["gla_wa2_b"][l]
    small[:, SM_CKV:SM_CKV + CTX] = w["cache_mla_ckv"][0, l].T
    small[64:96, SM_KR:SM_KR + CTX] = w["cache_mla_krope"][0, l].T
    for d in range(2):
        for h in range(G_HEADS):
            at = SM_ST + d * 256 + h * G_DV
            small[32 * h:32 * h + 32, at:at + G_DV] = w["state_gla"][0, l, d, h]
    rows = [w["b_mod"][l], w["norm1_g"][l], w["norm2_g"][l], w["mla_q_norm_g"][l], w["mla_kv_norm_g"][l],
            w["gla_ba_f"][l], w["gla_ba_b"][l], w["gla_norm_g"][l]]
    return np.stack(tiles), small, np.concatenate([r.reshape(-1, P).T for r in rows], 1)


def fm(a):
    return a.T.reshape(-1, P, a.shape[0]).transpose(1, 0, 2)


def kernel(**inputs):
    import concourse.bacc as bacc
    from concourse.bass_utils import run_bass_kernel_spmd

    w = {n: np.asarray(a) for n, a in inputs.items()}
    layers = [layer_inputs(w, l) for l in range(DEPTH)]
    table, dft, mask = constants()
    arrays = dict(
        xT=fm(np.concatenate([w["x_prompt"][0], w["x_sample"][0]], 0)),
        cond=fm(np.stack([w["c_ctx"], w["c"][0]])),
        stream=np.concatenate([s for s, _, _ in layers]), small=np.stack([s for _, s, _ in layers]),
        vecs=np.concatenate([v for _, _, v in layers] + [w["final_norm_g"].reshape(-1, P).T], 1),
        table=table, dft=dft, mask=mask)
    arrays = {f"in_{n}": np.ascontiguousarray(a) for n, a in arrays.items()}
    outs = dict(yT=[P, KT, TOK], ckvT=[DEPTH, P, CTX], krT=[DEPTH, ROPE, CTX], st=[DEPTH, P, 2, 256])
    nc = bacc.Bacc("TRN2", target_bir_lowering=False, num_devices=1)
    nc.disable_value_cache = True
    args = [nc.dram_tensor(n, a.shape, mybir.dt.from_np(a.dtype), kind="ExternalInput").ap() for n, a in arrays.items()]
    args += [nc.dram_tensor(f"out_{n}", s, F32, kind="ExternalOutput").ap() for n, s in outs.items()]
    build(nc, *args, links=LINKS)
    r = run_bass_kernel_spmd(nc, [arrays], core_ids=[0]).results[0]
    y = r["out_yT"].transpose(2, 1, 0).reshape(TOK, D)
    st = np.stack([r["out_st"][:, 32 * h:32 * h + 32, :, h * G_DV:(h + 1) * G_DV] for h in range(G_HEADS)], 1)
    return (y[None, :CTX], y[None, CTX:], r["out_ckvT"].transpose(0, 2, 1)[None], r["out_krT"].transpose(0, 2, 1)[None],
            st.transpose(0, 3, 1, 2, 4)[None])
```
